# Optimizing a Trainium2 kernel written in Bass

```python
import math, functools
import jax, jax.numpy as jnp
from jax import lax
import numpy as np

D_MODEL = 1024
BATCH = 1
SEQ = 256
DEPTH = 2
DEC_BATCH = 8
DEC_SEQ = 1
PAST_LEN = 256
PAGE_SIZE = 128

N_HEADS = 4
HEAD_DIM = 64
V_DIM = 2 * HEAD_DIM
QK_W = N_HEADS * 2 * HEAD_DIM
ATTN_W = N_HEADS * V_DIM
POOL_WINDOWS = (2, 4, 8, 16)
N_POOL_GROUPS = len(POOL_WINDOWS)
POOL_W = D_MODEL // 2
POOL_GROUP_W = POOL_W // N_POOL_GROUPS
POOL_BUF = max(POOL_WINDOWS) - 1
N_BRANCH = 2
IN_COLS = 2 * QK_W + ATTN_W + POOL_W + N_BRANCH * D_MODEL
N_BUCKETS = 32
MAX_DISTANCE = 128
D_FF = 2816
N_EXPERTS = 8
TOP_K = 2
D_EXPERT = 3584
N_DENSE = (DEPTH + 1) // 2
N_MOE = DEPTH // 2
Q_BLOCK = 128
EPS = 1e-6

kernel_name = "hybrid_diffattn_pool_gated_decoder_step"

F32 = jnp.float32

def rms_norm(x, gain):
    xf = x.astype(F32)
    y = xf * lax.rsqrt(jnp.mean(xf * xf, axis=-1, keepdims=True) + EPS)
    return (y * gain.astype(F32)).astype(x.dtype)

def lambda_init(layer):
    return 0.8 - 0.6 * math.exp(-0.3 * layer)

def diff_lambda_value(lp, layer):
    lp = lp.astype(F32)
    return (jnp.exp(jnp.sum(lp[0] * lp[1])) - jnp.exp(jnp.sum(lp[2] * lp[3]))
            + lambda_init(layer))

def t5_bucket(rel):
    n = jnp.maximum(rel, 0)
    max_exact = N_BUCKETS // 2
    nf = jnp.maximum(n, 1).astype(F32)
    large = max_exact + (jnp.log(nf / max_exact) / math.log(MAX_DISTANCE / max_exact)
                         * (N_BUCKETS - max_exact)).astype(jnp.int32)
    large = jnp.minimum(large, N_BUCKETS - 1)
    return jnp.where(n < max_exact, n, large)

def rel_bias_for(rel, rel_bias):
    return jnp.transpose(rel_bias.astype(F32)[t5_bucket(rel)], (2, 0, 1))

def in_proj(h, w_in_l, q_gain, k_gain):
    B, T = h.shape[:2]
    z = h @ w_in_l
    q, k, v, u, g = jnp.split(
        z, [QK_W, 2 * QK_W, 2 * QK_W + ATTN_W, 2 * QK_W + ATTN_W + POOL_W], axis=-1)
    q = rms_norm(q.reshape(B, T, N_HEADS, 2, HEAD_DIM), q_gain)
    k = rms_norm(k.reshape(B, T, N_HEADS, 2, HEAD_DIM), k_gain)
    v = v.reshape(B, T, N_HEADS, V_DIM)
    g = jax.nn.sigmoid(g.astype(F32)).astype(h.dtype).reshape(B, T, N_BRANCH, D_MODEL)
    return q, k, v, u, g

def attn_prompt(q, k, v, lam, rel_bias):
    B, S = q.shape[:2]
    nb = S // Q_BLOCK
    scale = HEAD_DIM ** -0.5
    kpos = jnp.arange(S)
    qb = jnp.moveaxis(q.reshape(B, nb, Q_BLOCK, N_HEADS, 2, HEAD_DIM), 1, 0)

    def block(args):
        i, qi = args
        qpos = i * Q_BLOCK + jnp.arange(Q_BLOCK)
        rel = qpos[:, None] - kpos[None, :]
        s = jnp.einsum('bqhmd,bkhmd->bmhqk', qi, k, preferred_element_type=F32) * scale
        s = jnp.where(rel >= 0, s + rel_bias_for(rel, rel_bias), -jnp.inf)
        p = jax.nn.softmax(s, axis=-1)
        a = (p[:, 0] - lam * p[:, 1]).astype(v.dtype)
        return jnp.einsum('bhqk,bkhe->bqhe', a, v)

    o = lax.map(block, (jnp.arange(nb), qb))
    return jnp.moveaxis(o, 0, 1).reshape(B, S, N_HEADS, V_DIM)

def attn_sample(q, k, v, lam, k_past, v_past, rel_bias):
    T = q.shape[1]
    P = k_past.shape[1]
    scale = HEAD_DIM ** -0.5
    qpos = P + jnp.arange(T)
    rel_past = qpos[:, None] - jnp.arange(P)[None, :]
    rel_new = qpos[:, None] - qpos[None, :]
    s_past = (jnp.einsum('bqhmd,bkhmd->bmhqk', q, k_past, preferred_element_type=F32) * scale
              + rel_bias_for(rel_past, rel_bias))
    s_new = jnp.einsum('bqhmd,bkhmd->bmhqk', q, k, preferred_element_type=F32) * scale
    s_new = jnp.where(rel_new >= 0, s_new + rel_bias_for(rel_new, rel_bias), -jnp.inf)
    p = jax.nn.softmax(jnp.concatenate([s_past, s_new], axis=-1), axis=-1)
    a = (p[:, 0] - lam * p[:, 1]).astype(v.dtype)
    return (jnp.einsum('bhqk,bkhe->bqhe', a[..., :P], v_past)
            + jnp.einsum('bhqk,bkhe->bqhe', a[..., P:], v))

def pool_mix(u, buf, pos0, w_pool_l, pool_scale_l):
    B, T = u.shape[:2]
    uf = u.astype(F32)
    ext = jnp.concatenate([buf.astype(F32), uf], axis=1)
    cs = jnp.concatenate([jnp.zeros((B, 1, POOL_W), F32), jnp.cumsum(ext, axis=1)], axis=1)
    pos = pos0 + jnp.arange(T)
    outs = []
    for gi, w in enumerate(POOL_WINDOWS):
        ch = slice(gi * POOL_GROUP_W, (gi + 1) * POOL_GROUP_W)
        win_sum = (cs[:, POOL_BUF + 1:POOL_BUF + 1 + T, ch]
                   - cs[:, POOL_BUF + 1 - w:POOL_BUF + 1 - w + T, ch])
        cnt = jnp.minimum(pos + 1, w).astype(F32)[None, :, None]
        outs.append(win_sum / cnt - uf[:, :, ch])
    d = jnp.stack(outs, axis=2)
    y = jnp.einsum('btgc,gce->btge', d, w_pool_l.astype(F32)).reshape(B, T, POOL_W)
    y = (y * pool_scale_l.astype(F32)).astype(u.dtype)
    return y, ext[:, -POOL_BUF:].astype(u.dtype)

def swiglu(h, wg, wu, wd):
    return (jax.nn.silu(h @ wg) * (h @ wu)) @ wd

def moe_swiglu(h, w_router, wg, wu, wd):
    logits = (h @ w_router).astype(F32)
    top_v, top_i = lax.top_k(logits, TOP_K)
    probs = jax.nn.softmax(top_v, axis=-1)
    comb = jnp.sum(jax.nn.one_hot(top_i, N_EXPERTS, dtype=F32) * probs[..., None], axis=-2)
    comb = comb.astype(h.dtype)
    out = jnp.zeros_like(h)
    for e in range(N_EXPERTS):
        out = out + comb[..., e:e + 1] * swiglu(h, wg[e], wu[e], wd[e])
    return out

def layer_forward(x, c, pool_buf, pos0, attend, layer, w_ada_l, b_ada_l, g_mix_l, g_ffn_l,
                  w_in_l, q_norm_l, k_norm_l, diff_lambda_l, subln_l, w_pool_l, pool_scale_l,
                  w_branch_l, w_out_l, ffn_w):
    mod = jax.nn.silu(c) @ w_ada_l + b_ada_l
    sh1, sc1, gt1, sh2, sc2, gt2 = [t[:, None, :] for t in jnp.split(mod, 6, axis=-1)]
    h = rms_norm(x, g_mix_l) * (1 + sc1) + sh1
    q, k, v, u, g = in_proj(h, w_in_l, q_norm_l, k_norm_l)
    lam = diff_lambda_value(diff_lambda_l, layer)
    o = attend(q, k, v, lam)
    o = rms_norm(o, subln_l) * (1.0 - lambda_init(layer))
    o = o.reshape(o.shape[0], o.shape[1], ATTN_W)
    y_pool, new_buf = pool_mix(u, pool_buf, pos0, w_pool_l, pool_scale_l)
    pa = o @ w_branch_l[:ATTN_W]
    pb = y_pool @ w_branch_l[ATTN_W:]
    merged = g[:, :, 0] * pa + g[:, :, 1] * pb
    x = x + gt1 * (merged @ w_out_l)
    h2 = rms_norm(x, g_ffn_l) * (1 + sc2) + sh2
    if layer % 2 == 0:
        f = swiglu(h2, *ffn_w)
    else:
        f = moe_swiglu(h2, *ffn_w)
    x = x + gt2 * f
    return x, k, v, new_buf

def setup_inputs(seed: int = 0) -> dict:
    key = jax.random.key(seed)
    ks = iter(jax.random.split(key, 40))

    def nrm(shape, scale):
        return jax.random.normal(next(ks), shape, F32) * scale

    n_pages = PAST_LEN // PAGE_SIZE
    n_used = DEC_BATCH * n_pages
    n_phys = n_used + max(1, n_used // 4)
    perm = jax.random.permutation(next(ks), n_phys)
    page_table = perm[:n_used].reshape(DEC_BATCH, n_pages).astype(jnp.int32)
    D = D_MODEL
    return {
        "x_prompt": nrm((BATCH, SEQ, D), 1.0),
        "x_sample": nrm((DEC_BATCH, DEC_SEQ, D), 1.0),
        "c_prompt": nrm((BATCH, D), 1.0),
        "c_sample": nrm((DEC_BATCH, D), 1.0),
        "cache_k": nrm((DEPTH, n_phys, PAGE_SIZE, N_HEADS, 2, HEAD_DIM), 1.0),
        "cache_v": nrm((DEPTH, n_phys, PAGE_SIZE, N_HEADS, V_DIM), 1.0),
        "state_pool": nrm((DEPTH, DEC_BATCH, POOL_BUF, POOL_W), 1.0),
        "page_table": page_table,
        "rel_bias": nrm((N_BUCKETS, N_HEADS), 0.5),
        "w_ada": nrm((DEPTH, D, 6 * D), 0.5 * D ** -0.5),
        "b_ada": nrm((DEPTH, 6 * D), 0.02),
        "g_mix": 1.0 + nrm((DEPTH, D), 0.02),
        "g_ffn": 1.0 + nrm((DEPTH, D), 0.02),
        "w_in": nrm((DEPTH, D, IN_COLS), D ** -0.5),
        "q_norm": 1.0 + nrm((DEPTH, 2, HEAD_DIM), 0.02),
        "k_norm": 1.0 + nrm((DEPTH, 2, HEAD_DIM), 0.02),
        "diff_lambda": nrm((DEPTH, 4, HEAD_DIM), 0.1),
        "subln": 1.0 + nrm((DEPTH, V_DIM), 0.02),
        "w_pool": nrm((DEPTH, N_POOL_GROUPS, POOL_GROUP_W, POOL_GROUP_W), POOL_GROUP_W ** -0.5),
        "pool_scale": 1.0 + nrm((DEPTH, POOL_W), 0.1),
        "w_branch": nrm((DEPTH, ATTN_W + POOL_W, D), (ATTN_W) ** -0.5),
        "w_out": nrm((DEPTH, D, D), D ** -0.5),
        "w_ff_gate": nrm((N_DENSE, D, D_FF), D ** -0.5),
        "w_ff_up": nrm((N_DENSE, D, D_FF), D ** -0.5),
        "w_ff_down": nrm((N_DENSE, D_FF, D), D_FF ** -0.5),
        "w_router": nrm((N_MOE, D, N_EXPERTS), D ** -0.5),
        "w_exp_gate": nrm((N_MOE, N_EXPERTS, D, D_EXPERT), D ** -0.5),
        "w_exp_up": nrm((N_MOE, N_EXPERTS, D, D_EXPERT), D ** -0.5),
        "w_exp_down": nrm((N_MOE, N_EXPERTS, D_EXPERT, D), D_EXPERT ** -0.5),
    }

def reference(x_prompt, x_sample, c_prompt, c_sample, cache_k, cache_v, state_pool, page_table,
              rel_bias, w_ada, b_ada, g_mix, g_ffn, w_in, q_norm, k_norm, diff_lambda, subln,
              w_pool, pool_scale, w_branch, w_out, w_ff_gate, w_ff_up, w_ff_down, w_router,
              w_exp_gate, w_exp_up, w_exp_down):
    B = x_prompt.shape[0]
    DB = x_sample.shape[0]
    past = page_table.shape[1] * PAGE_SIZE
    zero_buf = jnp.zeros((B, POOL_BUF, POOL_W), x_prompt.dtype)
    attend_p = functools.partial(attn_prompt, rel_bias=rel_bias)
    xp, xs = x_prompt, x_sample
    kp_l, vp_l, pp_l, ks_l, vs_l, ps_l = [], [], [], [], [], []
    for l in range(DEPTH):
        j = l // 2
        if l % 2 == 0:
            ffn_w = (w_ff_gate[j], w_ff_up[j], w_ff_down[j])
        else:
            ffn_w = (w_router[j], w_exp_gate[j], w_exp_up[j], w_exp_down[j])
        lw = (w_ada[l], b_ada[l], g_mix[l], g_ffn[l], w_in[l], q_norm[l], k_norm[l],
              diff_lambda[l], subln[l], w_pool[l], pool_scale[l], w_branch[l], w_out[l], ffn_w)
        xp, kp, vp, bp = layer_forward(xp, c_prompt, zero_buf, 0, attend_p, l, *lw)
        k_past = cache_k[l, page_table].reshape(DB, past, N_HEADS, 2, HEAD_DIM)
        v_past = cache_v[l, page_table].reshape(DB, past, N_HEADS, V_DIM)
        attend_s = functools.partial(attn_sample, k_past=k_past, v_past=v_past,
                                     rel_bias=rel_bias)
        xs, ks_, vs_, bs = layer_forward(xs, c_sample, state_pool[l], past, attend_s, l, *lw)
        kp_l.append(kp); vp_l.append(vp); pp_l.append(bp)
        ks_l.append(ks_); vs_l.append(vs_); ps_l.append(bs)
    new_k_prompt = jnp.stack(kp_l, axis=0)
    new_v_prompt = jnp.stack(vp_l, axis=0)
    new_pool_prompt = jnp.stack(pp_l, axis=0)
    new_k_sample = jnp.stack(ks_l, axis=0)
    new_v_sample = jnp.stack(vs_l, axis=0)
    new_pool_sample = jnp.stack(ps_l, axis=0)
    return (xp, xs, new_k_prompt, new_v_prompt, new_pool_prompt,
            new_k_sample, new_v_sample, new_pool_sample)


_drawn_inputs = setup_inputs


def setup_inputs(seed=0):
    import zlib

    import numpy as np

    out = dict(_drawn_inputs(seed))
    spreads = {}
    factors = {'g_mix': 2.958,
     'g_ffn': 4.344,
     'q_norm': 7.171,
     'k_norm': 3.015,
     'diff_lambda': 2.977,
     'subln': 6.955}
    for name, (base, spread) in spreads.items():
        noise = np.random.default_rng([zlib.crc32(name.encode()), seed]).standard_normal(out[name].shape)
        drawn = base * np.exp(spread * noise) if base else spread * noise
        out[name] = __import__('jax').numpy.asarray(drawn.astype(out[name].dtype))
    for name, factor in factors.items():
        out[name] = (out[name] * factor).astype(out[name].dtype)
    return out
```

```python
from collections import namedtuple
from contextlib import ExitStack

import numpy as np

import concourse.bass as bass
from concourse import mybir

F32 = mybir.dt.float32
I32 = mybir.dt.int32
ALU = mybir.AluOpType
ACT = mybir.ActivationFunctionType
AX = mybir.AxisListType

P = 128
LAYERS = 2
D = 1024
DC = D // P
S = 256
NS = 8
T = S + NS
NC = 1 + NS
H = 4
HD = 64
QC = 4
ZC = 16
GC = 16
EPS = 1e-6
WINDOWS = (2, 4, 8, 16)
BUF = 15
PAGE = 128
PAGES = 2
PHYS = 20
PAST = PAGE * PAGES
BUCKETS, MAXDIST = 32, 128
FF = 2816
FE = 3584
E = 8
CAP = 96
BODY = 7
BODIES = FE // P // BODY
FF_GROUPS = (6, 6, 5, 5)
RING = 18
ERING = 3 * BODY
SCALE = HD ** -0.5
LAM_INIT = [0.8 - 0.6 * float(np.exp(-0.3 * l)) for l in range(LAYERS)]
MASKED = -1.0e30
KV_RING = 4

WL = 384
_SIZES = [("ident", 128), ("halves", 128), ("ones", 128), ("before", 128), ("onehot_w", WL), ("onehot_s", PAST + 1),
          ("comb_a", 32), ("comb_b", 32), ("slot", CAP), ("first", 8), ("valid", 3), ("pick", NS * P), ("inv", 64), ("gather_c", NC)]
CO = {}
_at = 0
for _n, _s in _SIZES:
    CO[_n] = (_at, _at + _s)
    _at += _s
CW = _at


def bucket(n):
    half = BUCKETS // 2
    if n < half:
        return n
    return min(BUCKETS - 1, half + int(np.log(n / half) / np.log(MAXDIST / half) * (BUCKETS - half) + 1e-9))


def constants():
    c = np.zeros((P, CW), np.float32)

    def put(name, a):
        c[:a.shape[0], CO[name][0]:CO[name][0] + a.shape[1]] = a

    put("ident", np.eye(P))
    put("halves", np.kron(np.eye(2), np.ones((HD, HD))))
    put("ones", np.ones((P, P)))
    put("before", np.triu(np.ones((P, P)), 1))
    w = np.zeros((BUCKETS + 1, WL))
    for j in range(WL):
        rel = S - 1 - j
        w[bucket(rel) if rel >= 0 else BUCKETS, j] = 1
    put("onehot_w", w)
    s = np.zeros((BUCKETS + 1, PAST + 1))
    for j in range(PAST + 1):
        s[bucket(PAST - j), j] = 1
    put("onehot_s", s)
    for name, m in (("comb_a", 0), ("comb_b", 1)):
        a = np.zeros((64, 32))
        for b in range(NS):
            for h in range(H):
                a[b * 8 + h * 2 + m, h * 8 + b] = 1
        put(name, a)
    put("slot", np.tile(np.arange(CAP), (P, 1)))
    put("first", np.tile(np.arange(8, 0, -1), (P, 1)))
    v = np.ones((P, 3))
    v[NS:, 2] = 0
    put("valid", v)
    put("pick", np.repeat(np.eye(NS), P, axis=1))
    i = np.zeros((H, 16))
    for g, w_ in enumerate(WINDOWS):
        i[g] = 1.0 / np.minimum(np.arange(16) + 1, w_)
    put("inv", np.tile(i.reshape(1, 64), (P, 1)))
    put("gather_c", np.tile(np.eye(32)[:, :NC], (4, 1)))
    return c


class Step:

    def __init__(self, engine, sem):
        self.engine, self.sem, self.n = engine, sem, 0

    def __call__(self, instruction):
        self.n += 1
        instruction.then_inc(self.sem, 1)
        self.engine.wait_ge(self.sem, self.n)


def build(nc, A, O, const_in):
    ctx = ExitStack()
    with ctx:
        def sb(name, shape, dt=F32):
            return ctx.enter_context(nc.sbuf_tensor(name, shape, dt))

        def sem(name):
            return ctx.enter_context(nc.semaphore(name))

        bank = [ctx.enter_context(nc.psum_tensor(f"bank{i}", [P, 512], F32)) for i in range(8)]

        cst = sb("cst", [P, CW])
        ring = sb("ring", [P, RING, DC, P])
        xT = sb("xT", [P, DC, T])
        hT = sb("hT", [P, DC, T])
        sq = sb("sq", [P, DC, T])
        mod = sb("mod", [P, 48, NC])
        gain = sb("gain", [P, DC, NC])
        cT = sb("cT", [P, DC, 32])
        vecT = sb("vecT", [P, 142])
        bias = sb("bias", [P, H, S])
        bias_s = sb("bias_s", [64, PAST + 1])
        lam = sb("lam", [P, 4])
        neglam = sb("neglam", [P, LAYERS])
        sub_gain = sb("sub_gain", [P, LAYERS])
        state_sum = sb("state_sum", [P, LAYERS, H, NS])
        comb_m = sb("comb_m", [64, 32])
        eps = sb("eps", [P, 1])
        zero = sb("zero", [P, 1])
        zeros = sb("zeros", [P, 4 * CAP], mybir.dt.bfloat16)
        root = sb("root", [P, 2, T])
        inv = sb("inv", [P, T])
        w_pool = sb("w_pool", [P, H, P])
        w_route = sb("w_route", [P, DC, E])
        table = sb("table", [1, NS * PAGES], I32)
        AREA = 21800
        area = sb("area", [P, AREA])

        def layout(parts, at=0):
            out = {}
            for name, shape in parts:
                n = int(np.prod(shape[1:]))
                v = area[0:shape[0], at:at + n]
                if len(shape) == 3:
                    v = v.rearrange("p (a b) -> p a b", a=shape[1])
                elif len(shape) == 4:
                    v = v.rearrange("p (a b c) -> p a b c", a=shape[1], b=shape[2])
                out[name] = v
                at += n
            assert at <= AREA, at
            return out

        def const(name, rows=P):
            return cst[0:rows, CO[name][0]:CO[name][1]]

        ident, ones, halves, before = const("ident"), const("ones"), const("halves"), const("before")
        inv_count = const("inv").rearrange("p (g t) -> p g t", g=H)

        PRO = layout([("x_tok", [P, 2, D]), ("xs_tok", [NS, D]), ("c_tok", [NC, D]), ("c_act", [NC, D]),
                      ("vec_a", [112, P]), ("vec_b", [30, P]), ("rb", [BUCKETS + 1, H]),
                      ("rb_wide", [BUCKETS + 1, H, P]), ("rb_rows", [BUCKETS + 1, 64]),
                      ("lam_in", [P, 4, 2, HD]), ("lam_prod", [P, 4, HD]), ("bias_row", [P, H, WL]),
                      ("state_in", [NS * BUF, LAYERS, 512])])
        ATT = layout([("q_raw", [P, H, T]), ("qz", [P, 2, H, S]), ("q_s", [P, H, NS]), ("kT", [P, H, T]),
                      ("vT", [P, H, T]), ("u_ext", [P, H, BUF + S]), ("u_s", [P, H, NS]), ("u_last", [P, H, 23]),
                      ("yT", [P, H, T]), ("gate", [P, GC, T]), ("v_tok", [P, 2, 512]), ("k_tok", [P, 2, 512]),
                      ("ks_tok", [NS, 512]), ("vs_tok", [NS, 512]), ("u_tok", [23, 512]), ("qs_tok", [NS, 512]),
                      ("prob", [P, 4, S]), ("prob_s", [64, PAST + 1]), ("a", [P, 2, S]), ("aT", [P, 2, 384]),
                      ("kv", [P, KV_RING, 512]), ("prod", [P, 512]), ("raw_s", [P, 2, 64]),
                      ("new_s", [NS, NS]), ("new_d", [NS, NS, NS]), ("a_s", [P, 96]), ("new_wide", [64, P]),
                      ("top", [P, 4]), ("sum", [P, 4]), ("rec", [P, 4]), ("top_s", [64, 4]), ("tmp_s", [P, DC, NS])])
        oT = ATT["q_raw"]
        o_sq = ATT["prob"].rearrange("p a b -> p (a b)")[:, 0:2 * T].rearrange("p (a b) -> p a b", a=2)
        mod_rows = hT[:, :, :].rearrange("p a b -> p (a b)")[:, 0:2048].rearrange("p (a b) -> p a b", a=4)
        scr_a = sq[:, :, :].rearrange("p a b -> p (a b)")[:, 0:4 * 271].rearrange("p (g t) -> p g t", g=4)
        scr_b = sq[:, :, :].rearrange("p a b -> p (a b)")[:, 4 * 271:7 * 271].rearrange("p (g t) -> p g t", g=3)
        FFN = layout([("extra", [P, 3, D]), ("silu", [P, BODY, T]), ("act", [P, BODY, T]), ("fT", [P, DC, T]),
                      ("h_tok", [P, 3, D]), ("h_got", [P, DC, CAP]), ("y", [P, DC, CAP]), ("y_tok", [CAP, D]),
                      ("got", [P, 3, CAP]), ("got_w", [P, 3, CAP]), ("put", [CAP, T]), ("put_next", [CAP, T]), ("cmb_wide", [P, 3, P]),
                      ("cmb", [P, T]), ("logit", [P, 3, E]), ("rank", [P, 3, E + 1]), ("sel", [P, 3, E + 1]), ("wt", [P, 3, E + 1]),
                      ("one", [P, 3, E]), ("two", [P, 3, E]), ("key", [P, 3, E]), ("max", [P, 3, 4]), ("cur", [P, 3, 3]),
                      ("count", [P, E]), ("tmp_s", [P, DC, NS])])
        y_out = layout([("y_out", [P, 3, D])])["y_out"]
        count_i = sb("count_i", [P, E + 1], I32)
        extra = FFN["extra"]

        def slot(s):
            if s < RING:
                return ring[:, s, :, :]
            return extra[:, s - RING, :].rearrange("p (c n) -> p c n", c=DC)

        bias_dram = nc.dram_tensor("bias_rows", [P, H * WL], F32, kind="Internal").ap()

        names = """inputs_in tokens_in c_in mod_rows_out mod_mm zero_ready page_in_cache pages_used silu_c c_mm c_out x_mm x_out vec_mm vec_out wide_ready bias_mm bias_out
                 bias_wrote bias_in lam_exp lam_ready state_mm state_out ada_mm mod_out square_out sum_mm root_out h_ready
                 z_mm z_out gate_out qk_square qk_sum_mm qk_root qk_ready qs_mm ks_ready spread_mm raw_ready
                 v_mm v_out k_mm k_out vs_mm vs_out us_mm us_out score_mm score_out top_ready exp_out a_ready a_mm aT_out
                 av_mm o_out raw_s_mm raw_s_out top_s_ready exp_s_out prob_s_ready a_s_mm a_s_out av_s_mm o_s_out
                 o_square o_sum_mm o_root o_ready d_ready pool_mm y_ready branch_mm branch_out merged out_mm x_new
                 gate_mm up_mm silu_out act_out y_mm y_added n_mm f_zero f_ready h_tok_mm h_tok_out route_mm logits_out
                 sel_ready rank_mm routed got_ready h_got_mm h_got_out put_mm put_out yT_mm yT_out y_tok_mm y_tok_out
                 put_y_mm f_added expert_done cmb_wide_ready cmb_mm cmb_out final_mm final_out stored dve_step act_step
                 kv_used w_pool_in pooled cur_ready put_kept got_one act_raw exp_two v_out_u""".split()
        s = namedtuple("Semaphores", names)(*[sem(name) for name in names])
        page_in = [sem(f"page_in_{i}") for i in range(ERING)]
        kv_in = [sem(f"kv_in_{i}") for i in range(KV_RING)]

        block = ctx.enter_context(nc.Block())

        INPUTS = 16 * 11
        LAYER_PAGES = 48 + 32 + 8 + 8
        FF_PAGES = 3 * FF // P
        DENSE_CHUNKS = FF // P
        STRAIGHT = LAYERS * LAYER_PAGES + FF_PAGES
        assert FF_PAGES % RING == FF_PAGES - 3 * RING and (LAYER_PAGES + FF_PAGES) % RING == 0
        landed = [16 * len(range(i, STRAIGHT, RING)) for i in range(RING)] + [0] * 3
        eslot = [(STRAIGHT + i) % RING for i in range(RING)] + [RING, RING + 1, RING + 2]

        def cols(w, j):
            return w[:, j * P:(j + 1) * P].rearrange("(c p) n -> p c n", p=P)

        def layer_pages(l):
            for j in range(16):
                yield cols(A["w_ada"][l], j)
            for j in range(32):
                yield cols(A["w_in"][l], j)
            for j in range(16, 48):
                yield cols(A["w_ada"][l], j)
            for j in range(8):
                yield cols(A["w_branch"][l], j)
            for j in range(8):
                yield cols(A["w_out"][l], j)
            if l == 0:
                at = 0
                for n in FF_GROUPS:
                    for j in range(at, at + n):
                        yield cols(A["w_ff_gate"][0], j)
                        yield cols(A["w_ff_up"][0], j)
                    for j in range(at, at + n):
                        yield A["w_ff_down"][0][j * P:(j + 1) * P, :].rearrange("p (c n) -> p c n", c=DC)
                    at += n

        def layer_page(l):
            return l * (LAYER_PAGES + FF_PAGES)

        def experts(dve, step, f, act_t, silu):
            F = FFN
            for i in range(3):
                rows = min(P, T - i * P)
                for half in range(2):
                    n = 2 * i + half
                    dve.wait_ge(s.h_tok_mm, n + 1)
                    dve.tensor_copy(F["h_tok"][0:rows, i, half * 512:(half + 1) * 512], bank[4 + n % 2][0:rows, :]).then_inc(s.h_tok_out, 1)
            step(dve.memset(F["logit"], 0.0))
            for name in ("rank", "sel", "wt"):
                step(dve.memset(F[name][:, :, E:E + 1], 0.0))
            step(dve.memset(count_i[:, E:E + 1], 0))
            dve.wait_ge(s.route_mm, 1)
            step(dve.tensor_copy(F["logit"][:, 0:2, :], bank[6][:, 0:2 * E].rearrange("p (i e) -> p i e", i=2)))
            step(dve.tensor_copy(F["logit"][0:NS, 2, :], bank[6][0:NS, 2 * E:3 * E]))
            logit, key, m = F["logit"], F["key"], F["max"]
            order = const("first").unsqueeze(1).broadcast_to([P, 3, E])

            def at(j):
                return m[:, :, j:j + 1]

            def choose(j, one):
                step(dve.tensor_reduce(at(j), logit, AX.X, ALU.max))
                step(dve.tensor_tensor(key, logit, at(j).to_broadcast([P, 3, E]), ALU.is_equal))
                step(dve.tensor_tensor(key, key, order, ALU.mult))
                step(dve.tensor_reduce(at(2), key, AX.X, ALU.max))
                step(dve.tensor_tensor(one, key, at(2).to_broadcast([P, 3, E]), ALU.is_equal))

            choose(0, F["one"])
            step(dve.scalar_tensor_tensor(out=logit, in0=F["one"], scalar=-3.0e38, in1=logit, op0=ALU.mult, op1=ALU.add))
            choose(1, F["two"])
            step(dve.tensor_tensor(at(2), at(1), at(0), ALU.subtract))
            dve.tensor_copy(at(3), at(2)).then_inc(s.logits_out, 1)
            dve.wait_ge(s.exp_two, 1)
            step(dve.tensor_scalar(at(2), at(3), 1.0, None, ALU.add))
            step(dve.reciprocal(at(0), at(2)))
            step(dve.tensor_tensor(at(1), at(3), at(0), ALU.mult))
            valid = const("valid").unsqueeze(2)
            step(dve.tensor_tensor(at(0), at(0), valid, ALU.mult))
            step(dve.tensor_tensor(at(1), at(1), valid, ALU.mult))
            step(dve.tensor_tensor(F["wt"][:, :, 0:E], F["one"], at(0).to_broadcast([P, 3, E]), ALU.mult))
            step(dve.tensor_tensor(key, F["two"], at(1).to_broadcast([P, 3, E]), ALU.mult))
            step(dve.tensor_tensor(F["wt"][:, :, 0:E], F["wt"][:, :, 0:E], key, ALU.add))
            step(dve.tensor_tensor(F["sel"][:, :, 0:E], F["one"], F["two"], ALU.add))
            dve.tensor_tensor(F["sel"][:, :, 0:E], F["sel"][:, :, 0:E], valid.to_broadcast([P, 3, E]), ALU.mult).then_inc(s.sel_ready, 1)
            dve.wait_ge(s.rank_mm, 1)
            step(dve.tensor_copy(F["rank"][:, :, 0:E], bank[7][:, 0:3 * E].rearrange("p (i e) -> p i e", i=3)))
            dve.tensor_copy(count_i[:, 0:E], bank[7][:, 3 * E:4 * E]).then_inc(s.routed, 1)
            dve.wait_ge(s.routed, 1)
            dve.wait_ge(s.f_added, 1)

            cur = F["cur"]

            def make(e):
                if not isinstance(e, int):
                    dve.wait_ge(s.got_ready, e)
                for i, src in enumerate(("rank", "sel", "wt")):
                    column = F[src][:, :, e:e + 1] if isinstance(e, int) else F[src][:, :, bass.ds(e, 1)]
                    dve.tensor_copy(cur[:, :, i:i + 1], column).then_inc(s.cur_ready, 1)
                dve.wait_ge(s.cur_ready, e * 3 + 3)
                for i in range(3):
                    dve.tensor_scalar(F["got"][:, i, :], const("slot"), cur[:, i, 0:1], cur[:, i, 1:2],
                                      ALU.is_equal, ALU.mult).then_inc(s.got_one, 1)
                dve.tensor_copy(F["cmb_wide"], cur[:, :, 2:3].to_broadcast([P, 3, P])).then_inc(s.got_one, 1)
                dve.wait_ge(s.got_one, e * 4 + 4)
                dve.tensor_tensor(F["got_w"], F["got"], cur[:, :, 2:3].to_broadcast([P, 3, CAP]), ALU.mult).then_inc(s.got_ready, 1)

            def read_prepared(e, count):
                with dve.If(count < CAP + 1):
                    for half in range(2):
                        dve.wait_ge(s.h_got_mm, e * 2 + half + 1)
                        dve.tensor_copy(F["h_got"][:, 4 * half:4 * half + 4, :],
                                        bank[6 + half][:, 0:4 * CAP].rearrange("p (c n) -> p c n", c=4)).then_inc(s.h_got_out, 1)
                    dve.wait_ge(s.put_mm, e + 1)
                    dve.tensor_copy(F["put_next"], bank[2][0:CAP, 0:T]).then_inc(s.put_out, 1)
                with dve.Else():
                    dve.wait_ge(s.put_mm, e + 1)
                    dve.tensor_copy(F["cmb"], bank[2][:, 0:T]).then_inc(s.put_out, 1)
                    dve.sem_inc(s.h_got_out, 2)

            def keep_put(e):
                dve.wait_ge(s.put_out, e + 1)
                dve.tensor_copy(F["put"], F["put_next"]).then_inc(s.put_kept, 1)

            def load_count(e):
                return dve.value_load(count_i[0:1, bass.ds(e, 1)], min_val=0, max_val=T)

            step(dve.memset(F["put_next"], 0.0))
            make(0)
            read_prepared(0, dve.value_load(count_i[0:1, 0:1], min_val=0, max_val=T))
            keep_put(0)
            with dve.Fori(0, E) as e:
                count = load_count(e)
                make(e + 1)
                with dve.Fori(0, BODIES) as b:
                    n = e * BODIES + b
                    k = n * BODY + DENSE_CHUNKS
                    adds = n * DC + len(FF_GROUPS) * DC
                    with dve.If(count < CAP + 1):
                        dve.wait_ge(s.pages_used, n * ERING + STRAIGHT)
                        for c in range(BODY):
                            dve.wait_ge(s.silu_out, k + (c + 1))
                            dve.wait_ge(s.pages_used, n * ERING + (STRAIGHT + 2 * c + 2))
                            dve.tensor_tensor(act_t[:, c, 0:CAP], bank[2 + c % 2][:, 0:CAP], silu[:, c, 0:CAP],
                                              ALU.mult).then_inc(s.act_out, 1)
                        dve.sem_inc(s.y_added, DC)
                        dve.sem_inc(s.act_raw, BODY)
                    with dve.Else():
                        dve.wait_ge(s.pages_used, n * ERING + STRAIGHT)
                        for c in range(BODY):
                            dve.wait_ge(s.silu_out, k + (c + 1))
                            dve.wait_ge(s.pages_used, n * ERING + (STRAIGHT + 2 * c + 2))
                            dve.tensor_tensor(act_t[:, c, :], bank[2 + c % 2][:, 0:T], silu[:, c, :], ALU.mult).then_inc(s.act_raw, 1)
                            dve.wait_ge(s.act_raw, n * BODY + (c + 1))
                            dve.wait_ge(s.put_out, e + 1)
                            dve.tensor_tensor(act_t[:, c, :], act_t[:, c, :], F["cmb"], ALU.mult).then_inc(s.act_out, 1)
                        for j in range(DC):
                            if j < DC - 1:
                                dve.wait_ge(s.y_mm, n * (DC - 1) + (len(FF_GROUPS) * (DC - 1) + j + 1))
                            else:
                                dve.wait_ge(s.pages_used, n * ERING + (STRAIGHT + ERING))
                            dve.wait_ge(s.y_added, adds + j)
                            dve.wait_ge(s.f_added, e * DC + 1)
                            dve.tensor_tensor(f[:, j, :], bank[4 + j % 4][:, 0:T], f[:, j, :], ALU.add).then_inc(s.y_added, 1)
                with dve.If(count < CAP + 1):
                    for half in range(2):
                        dve.wait_ge(s.pages_used, e * (BODIES * ERING) + (STRAIGHT + BODIES * ERING))
                        dve.tensor_copy(F["y"][:, 4 * half:4 * half + 4, :],
                                        bank[4 + half][:, 0:4 * CAP].rearrange("p (c n) -> p c n", c=4)).then_inc(s.yT_out, 1)
                with dve.Else():
                    dve.wait_ge(s.act_out, (e + 1) * (BODIES * BODY) + DENSE_CHUNKS)
                    dve.sem_inc(s.yT_out, 2)
                read_prepared(e + 1, load_count(e + 1))
                with dve.If(count < CAP + 1):
                    for half in range(2):
                        dve.wait_ge(s.yT_mm, e * 2 + half + 1)
                        dve.tensor_copy(F["y_tok"][:, half * 512:(half + 1) * 512], bank[half][0:CAP, :]).then_inc(s.y_tok_out, 1)
                    dve.wait_ge(s.y_added, e * (BODIES * DC) + (len(FF_GROUPS) * DC + BODIES * DC))
                    for c in range(DC):
                        dve.wait_ge(s.put_y_mm, e * DC + c + 1)
                        dve.wait_ge(s.f_added, e * DC + (c + 1))
                        dve.tensor_tensor(f[:, c, :], bank[6 + c % 2][:, 0:T], f[:, c, :], ALU.add).then_inc(s.f_added, 1)
                with dve.Else():
                    dve.wait_ge(s.y_added, e * (BODIES * DC) + (len(FF_GROUPS) * DC + BODIES * DC))
                    dve.sem_inc(s.y_tok_out, 2)
                    dve.sem_inc(s.f_added, DC)
                keep_put(e + 1)
            dve.wait_ge(s.f_added, E * DC + 1)
            dve.wait_ge(s.y_added, E * BODIES * DC + len(FF_GROUPS) * DC)

        @block.sync
        def _(sp):
            n = 0
            for l in range(LAYERS):
                for src in layer_pages(l):
                    if n >= RING:
                        sp.wait_ge(s.pages_used, n - RING + 1)
                    sp.dma_start(slot(n % RING), src).then_inc(page_in[n % RING], 16)
                    n += 1
            with sp.Fori(0, E) as e:
                with sp.Fori(0, BODIES) as b:
                    for i in range(ERING):
                        if i >= RING:
                            sp.wait_ge(s.x_new, 3 * DC)
                            sp.wait_ge(s.pooled, LAYERS)
                            sp.wait_ge(s.pages_used, (e * BODIES + b) * ERING + (STRAIGHT - ERING + i + 1))
                        else:
                            sp.wait_ge(s.pages_used, (e * BODIES + b) * ERING + (STRAIGHT - RING + i + 1))
                        col = (b * BODY + (i // 2 if i < 2 * BODY else i - 2 * BODY)) * P
                        if i < 2 * BODY:
                            w = (A["w_exp_gate"], A["w_exp_up"])[i % 2][0]
                            src = w[bass.ds(e, 1), :, bass.ds(col, P)].rearrange("e (c p) n -> p (e c) n", p=P)
                        else:
                            src = A["w_exp_down"][0][bass.ds(e, 1), bass.ds(col, P), :].rearrange(
                                "e p (c n) -> (e p) c n", c=DC)
                        sp.dma_start(slot(eslot[i]), src).then_inc(page_in[eslot[i]], 16)

        @block.gpsimd
        def _(pool):
            rows = PRO["vec_a"], PRO["vec_b"]
            for dst, src in (
                    (rows[0][0:96, :], A["b_ada"].rearrange("l (j p) -> (l j) p", p=P)),
                    (rows[0][96:112, :], A["g_mix"].rearrange("l (j p) -> (l j) p", p=P)),
                    (rows[1][0:16, :], A["g_ffn"].rearrange("l (j p) -> (l j) p", p=P)),
                    (rows[1][16:24, :], A["pool_scale"].rearrange("l (j p) -> (l j) p", p=P)),
                    (rows[1][24:26, :], A["subln"]),
                    (rows[1][26:28, :], A["q_norm"].rearrange("l m d -> l (m d)")),
                    (rows[1][28:30, :], A["k_norm"].rearrange("l m d -> l (m d)")),
                    (PRO["rb"][0:BUCKETS, :], A["rel_bias"]),
                    (PRO["lam_in"].rearrange("p a b d -> p (a b d)"), A["diff_lambda"].rearrange("l a d -> (l a d)").partition_broadcast(P)),
                    (PRO["state_in"], A["state_pool"].rearrange("l b r c -> (b r) l c")),
                    (table[:, :], A["page_table"].rearrange("(a b) j -> a (b j)", a=1))):
                pool.dma_start(dst, src).then_inc(s.inputs_in, 16)
            pool.wait_ge(s.inputs_in, INPUTS)
            page = [pool.value_load(table[0:1, i:i + 1], min_val=0, max_val=PHYS - 1) for i in range(NS * PAGES)]

            stores = 0
            for l in range(LAYERS):
                for b in range(NS):
                    pool.dma_start(O[7][l, b:b + 1, 0:BUF - 1, :], A["state_pool"][l, b:b + 1, 1:BUF, :]).then_inc(s.stored, 16)
                    stores += 1

            pool.wait_ge(s.bias_out, H)
            pool.dma_start(bias_dram, PRO["bias_row"].rearrange("p h j -> p (h j)")).then_inc(s.bias_wrote, 16)
            pool.wait_ge(s.bias_wrote, 16)
            skew = bass.AP(tensor=bias_dram.tensor, offset=P - 1, ap=[[H * WL - 1, P], [WL, H], [1, S]])
            pool.dma_start(bias[:, :, :], skew).then_inc(s.bias_in, 16)

            n = 0
            for l in range(LAYERS):
                if l:
                    pool.wait_ge(s.pool_mm, H * l)
                    pool.wait_ge(s.x_new, 2 * DC * l)
                pool.dma_start(w_pool[:, :, :], A["w_pool"][l].rearrange("g c e -> c g e")).then_inc(s.w_pool_in, 16)
                if l == 0:
                    pool.wait_ge(s.h_ready, DC)
                    pool.wait_ge(s.state_out, LAYERS)
                    pool.wait_ge(s.bias_in, 16)
                def load(src, i, n):
                    if n >= KV_RING:
                        pool.wait_ge(s.kv_used, n - KV_RING + 1)
                    pool.dma_start(ATT["kv"][:, n % KV_RING, :], src).then_inc(kv_in[n % KV_RING], 16)
                for i in range(NS * PAGES):
                    load(A["cache_k"][l][bass.ds(page[i], 1)].rearrange("o p h m d -> (o p) (h m d)"), i, n)
                    n += 1
                for i in range(NS * PAGES):
                    if i == KV_RING:
                        pool.wait_ge(s.vs_out, l + 1)
                        pool.wait_ge(s.us_out, l + 1)
                        pool.wait_ge(s.v_out, 2 * (l + 1))
                        pool.wait_ge(s.k_out, 2 * (l + 1))
                        pool.wait_ge(s.ks_ready, l + 1)
                        for dst, src in (
                                (O[2][l, 0].rearrange("(i p) h m d -> p i (h m d)", p=P), ATT["k_tok"]),
                                (O[3][l, 0].rearrange("(i p) h e -> p i (h e)", p=P), ATT["v_tok"]),
                                (O[4][l, 0], ATT["u_tok"][0:BUF, :]),
                                (O[5][l].rearrange("b t h m d -> (b t) (h m d)"), ATT["ks_tok"]),
                                (O[6][l].rearrange("b t h e -> (b t) (h e)"), ATT["vs_tok"]),
                                (O[7][l, :, BUF - 1, :], ATT["u_tok"][BUF:BUF + NS, :])):
                            pool.dma_start(dst, src).then_inc(s.stored, 16)
                            stores += 1
                    load(A["cache_v"][l][bass.ds(page[i], 1)].rearrange("o p h e -> (o p) (h e)"), i, n)
                    n += 1
                pool.wait_ge(s.stored, 16 * stores)
                pool.sem_inc(s.pooled, 1)
            pool.wait_ge(s.final_out, 6)
            pool.dma_start(O[0][0].rearrange("(i p) d -> p i d", p=P), y_out[:, 0:2, :]).then_inc(s.stored, 16)
            pool.dma_start(O[1].rearrange("b t d -> (b t) d"), y_out[0:NS, 2, :]).then_inc(s.stored, 16)
            stores += 2
            pool.wait_ge(s.stored, 16 * stores)

        @block.scalar
        def _(act):
            act.dma_start(PRO["c_tok"][0:1, :], A["c_prompt"]).then_inc(s.c_in, 16)
            act.dma_start(PRO["c_tok"][1:NC, :], A["c_sample"]).then_inc(s.c_in, 16)
            act.dma_start(cst[:, :], const_in).then_inc(s.c_in, 16)
            act.dma_start(PRO["x_tok"], A["x_prompt"][0].rearrange("(i p) d -> p i d", p=P)).then_inc(s.tokens_in, 16)
            act.dma_start(PRO["xs_tok"], A["x_sample"].rearrange("b t d -> (b t) d")).then_inc(s.tokens_in, 16)
            act.dma_start(w_route[:, :, :], A["w_router"][0].rearrange("(c p) e -> p c e", p=P)).then_inc(s.tokens_in, 16)
            act.wait_ge(s.c_in, 16 * 3)
            act.activation(PRO["c_act"], PRO["c_tok"], ACT.Silu).then_inc(s.silu_c, 1)

            def read_rows(first, n, banks, at):
                for q in range(n // 4):
                    act.wait_ge(s.pages_used, first + 4 * (q + 1))
                    if q >= 4:
                        act.wait_ge(s.mod_mm, at + q - 3)
                    act.copy(mod_rows[:, q % 4, :], bank[banks[q % 2]][:, :]).then_inc(s.mod_rows_out, 1)

            read_rows(0, 16, (2, 3), 0)
            act.wait_ge(s.lam_ready, 1)
            act.activation(lam[:, :], lam[:, :], ACT.Exp).then_inc(s.lam_exp, 1)

            def norm(n):
                act.wait_ge(s.x_new, DC * n) if n else act.wait_ge(s.x_out, DC)
                act.activation(sq[:, :, :], xT[:, :, :], ACT.Square).then_inc(s.square_out, 1)
                act.wait_ge(s.sum_mm, n + 1)
                if n:
                    act.wait_ge(s.h_ready, DC * n)
                if n % 2:
                    act.wait_ge(s.o_ready, 2 * (n + 1))
                act.activation(root[:, 0, :], bank[1][:, 0:T], ACT.Sqrt, bias=eps[:, 0:1], scale=1.0 / D).then_inc(s.root_out, 1)

            for l in range(LAYERS):
                if l == 0:
                    act.wait_ge(s.wide_ready, 1)
                else:
                    act.wait_ge(s.x_new, 2 * DC * l)
                    read_rows(layer_page(l), 16, (2, 3), 12 * l)
                norm(2 * l)
                act.wait_ge(s.h_ready, DC * 2 * l + DC)
                for i in range(8):
                    act.wait_ge(s.z_out, ZC * l + i + 1)
                    raw = ATT["q_raw"][:, i, :] if i < QC else ATT["kT"][:, i - QC, :]
                    act.activation(sq[:, i, :], raw, ACT.Square).then_inc(s.qk_square, 1)
                for i in range(8):
                    act.wait_ge(s.qk_sum_mm, 8 * l + i + 1)
                    if i >= 2:
                        act.wait_ge(s.qk_ready, 8 * l + i - 1)
                    act.activation(root[:, i % 2, :], bank[6 + i % 2][:, 0:T], ACT.Sqrt,
                                   bias=eps[:, 0:1], scale=1.0 / HD).then_inc(s.qk_root, 1)
                for g in range(GC):
                    act.wait_ge(s.pages_used, layer_page(l) + 16 + ZC + g + 1)
                    act.activation(ATT["gate"][:, g, :], bank[2 + g % 4][:, 0:T], ACT.Sigmoid).then_inc(s.gate_out, 1)
                if l:
                    act.wait_ge(s.pooled, l)
                for i in range(2):
                    act.wait_ge(s.k_mm, 2 * l + i + 1)
                    act.copy(ATT["k_tok"][:, i, :], bank[6 + i][:, :]).then_inc(s.k_out, 1)
                for n in range(8):
                    w = P * (1 + n % 2)
                    prob = ATT["prob"][:, 2 * (n % 2):2 * (n % 2) + 2, 0:w]
                    top, total = ATT["top"][:, 2 * (n % 2):2 * (n % 2) + 2], ATT["sum"][:, 2 * (n % 2):2 * (n % 2) + 2]
                    act.wait_ge(s.top_ready, 8 * l + n + 1)
                    if n >= 2:
                        act.wait_ge(s.a_ready, 8 * l + n - 1)
                    for m in range(2):
                        act.activation(prob[:, m, :], prob[:, m, :], ACT.Exp, bias=top[:, m:m + 1], scale=1.0,
                                       accum_out=total[:, m:m + 1]).then_inc(s.exp_out, 1)
                    if n == 3:
                        act.wait_ge(s.top_s_ready, l + 1)
                        act.activation(ATT["prob_s"], ATT["prob_s"], ACT.Exp, bias=ATT["top_s"][:, 1:2], scale=1.0,
                                       accum_out=ATT["top_s"][:, 2:3]).then_inc(s.exp_s_out, 1)
                        read_rows(layer_page(l) + 48, 32, (1, 6), 12 * l + 4)
                    if n >= 4:
                        h = n - 4
                        act.wait_ge(s.a_mm, 4 * l + h + 1)
                        if h >= 2:
                            act.wait_ge(s.av_mm, 4 * l + h - 1)
                        act.copy(ATT["aT"][:, h % 2, :], bank[h % 2][:, 0:384]).then_inc(s.aT_out, 1)
                act.wait_ge(s.o_s_out, l + 1)
                act.wait_ge(s.o_out, 4 * (l + 1))
                for h in range(H):
                    if h >= 2:
                        act.wait_ge(s.o_sum_mm, 4 * l + h - 1)
                    act.activation(o_sq[:, h % 2, :], oT[:, h, :], ACT.Square).then_inc(s.o_square, 1)
                for h in range(H):
                    act.wait_ge(s.o_sum_mm, 4 * l + h + 1)
                    if h >= 2:
                        act.wait_ge(s.o_ready, 4 * l + h - 1)
                    act.activation(root[:, h % 2, :], bank[4 + h % 2][:, 0:T], ACT.Sqrt, bias=eps[:, 0:1],
                                   scale=1.0 / P).then_inc(s.o_root, 1)
                for g in range(H):
                    act.wait_ge(s.pool_mm, 4 * l + g + 1)
                    act.activation(ATT["yT"][:, g, :], bank[g % 2][:, 0:T], ACT.Identity, bias=zero[:, 0:1],
                                   scale=vecT[:, 128 + 4 * l + g:129 + 4 * l + g]).then_inc(s.y_ready, 1)
                norm(2 * l + 1)
                if l == 0:
                    k, at = 0, LAYER_PAGES
                    for n in FF_GROUPS:
                        for c in range(n):
                            act.wait_ge(s.pages_used, at + 2 * c + 1)
                            if c == 0:
                                act.wait_ge(s.act_out, k) if k else act.wait_ge(s.pooled, 1)
                            act.activation(FFN["silu"][:, c, :], bank[c % 2][:, 0:T], ACT.Silu).then_inc(s.silu_out, 1)
                            k += 1
                        at += 3 * n
                else:
                    act.wait_ge(s.pooled, LAYERS)
                    act.wait_ge(s.logits_out, 1)
                    act.activation(FFN["max"][:, :, 3:4], FFN["max"][:, :, 3:4], ACT.Exp).then_inc(s.exp_two, 1)
                    act.wait_ge(s.routed, 1)
                    with act.Fori(0, E) as e:
                        count = act.value_load(count_i[0:1, bass.ds(e, 1)], min_val=0, max_val=T)
                        with act.Fori(0, BODIES) as b:
                            k = (e * BODIES + b) * BODY
                            with act.If(count < CAP + 1):
                                for c in range(BODY):
                                    act.wait_ge(s.pages_used, (e * BODIES + b) * ERING + (STRAIGHT + 2 * c + 1))
                                    if c == 0:
                                        act.wait_ge(s.act_out, k + DENSE_CHUNKS)
                                    act.activation(FFN["silu"][:, c, 0:CAP], bank[c % 2][:, 0:CAP], ACT.Silu).then_inc(s.silu_out, 1)
                            with act.Else():
                                for c in range(BODY):
                                    act.wait_ge(s.pages_used, (e * BODIES + b) * ERING + (STRAIGHT + 2 * c + 1))
                                    if c == 0:
                                        act.wait_ge(s.act_out, k + DENSE_CHUNKS)
                                    act.activation(FFN["silu"][:, c, :], bank[c % 2][:, 0:T], ACT.Silu).then_inc(s.silu_out, 1)

        @block.tensor
        def _(pe):
            used = [0]

            def page():
                i = used[0] % RING
                pe.wait_ge(page_in[i], 16 * (used[0] // RING + 1))
                used[0] += 1
                return slot(i)

            def column(out, w, x):
                for c in range(DC):
                    mm = pe.matmul(out, w[:, c, :], x[:, c, :], start=(c == 0), stop=(c == DC - 1))
                mm.then_inc(s.pages_used, 1)

            def modulation(b, n, banks, at):
                def turn_rows(q):
                    pe.wait_ge(s.mod_rows_out, at + q + 1)
                    for t in range(4):
                        mm = pe.matmul(bank[b][:, NC * (4 * q + t):NC * (4 * q + t) + NC],
                                       mod_rows[:, q % 4, t * P:(t + 1) * P], const("gather_c"), start=True, stop=True)
                    mm.then_inc(s.mod_mm, 1)

                for q in range(n // 4):
                    if q >= 2:
                        pe.wait_ge(s.mod_rows_out, at + q - 1)
                    for t in range(4):
                        w = page()
                        for c in range(DC):
                            g = 32 * (c % 4)
                            mm = pe.matmul(bank[banks[q % 2]][g:g + 32, t * P:(t + 1) * P], cT[:, c, :], w[:, c, :],
                                           start=(c < 4), stop=(c >= 4), skip_group_check=True)
                        mm.then_inc(s.pages_used, 1)
                    if q:
                        turn_rows(q - 1)
                turn_rows(n // 4 - 1)

            pe.wait_ge(s.c_in, 16 * 3)
            pe.wait_ge(s.silu_c, 1)
            for c in range(DC):
                t = pe.transpose(bank[1][:, NC * c:NC * c + NC], PRO["c_act"][:, c * P:(c + 1) * P], ident[0:NC, 0:NC])
            t.then_inc(s.c_mm, 1)
            pe.wait_ge(s.c_out, 1)
            modulation(0, 16, (2, 3), 0)
            pe.wait_ge(s.inputs_in, INPUTS)
            pe.wait_ge(s.tokens_in, 16 * 3)
            pe.transpose(bank[1][:, 0:112], PRO["vec_a"], ident[0:112, 0:112])
            pe.transpose(bank[1][:, 112:142], PRO["vec_b"], ident[0:30, 0:30]).then_inc(s.vec_mm, 1)
            for c in range(DC):
                if c >= 4:
                    pe.wait_ge(s.x_out, c - 3)
                for i in range(2):
                    pe.transpose(bank[2 + c % 4][:, i * P:(i + 1) * P], PRO["x_tok"][:, i, c * P:(c + 1) * P], ident)
                pe.transpose(bank[2 + c % 4][:, S:T], PRO["xs_tok"][:, c * P:(c + 1) * P], ident[0:NS, 0:NS]).then_inc(s.x_mm, 1)
            pe.wait_ge(s.wide_ready, 1)
            for h in range(H):
                if h >= 2:
                    pe.wait_ge(s.bias_out, h - 1)
                pe.matmul(bank[6 + h % 2][:, 0:WL], PRO["rb_wide"][:, h, :], const("onehot_w", BUCKETS + 1),
                          start=True, stop=True).then_inc(s.bias_mm, 1)
            pe.wait_ge(s.vec_out, 1)
            pe.matmul(bank[1][0:64, 0:PAST + 1], PRO["rb_rows"], const("onehot_s", BUCKETS + 1),
                      start=True, stop=True).then_inc(s.bias_mm, 1)
            for l in range(LAYERS):
                pe.wait_ge(s.x_out, DC)
                for g in range(H):
                    t = pe.transpose(bank[4 + l][:, g * 120:(g + 1) * 120], PRO["state_in"][:, l, g * P:(g + 1) * P],
                                     ident[0:120, 0:120])
                t.then_inc(s.state_mm, 1)

            def sums(n):
                pe.wait_ge(s.square_out, n + 1)
                for c in range(DC):
                    mm = pe.matmul(bank[1][:, 0:T], ones, sq[:, c, :], start=(c == 0), stop=(c == DC - 1))
                mm.then_inc(s.sum_mm, 1)

            for l in range(LAYERS):
                if l == 0:
                    pe.wait_ge(s.state_out, LAYERS)
                    pe.wait_ge(s.bias_out, H + 1)
                else:
                    pe.wait_ge(s.x_new, 2 * DC * l)
                    modulation(0, 16, (2, 3), 12 * l)
                sums(2 * l)

                def z(i):
                    b = 2 + i % 4
                    k = i - 4
                    if k >= ZC:
                        pe.wait_ge(s.gate_out, GC * l + k - ZC + 1)
                    elif k >= 0:
                        pe.wait_ge(s.z_out, ZC * l + k + 1)
                    w = page()
                    for c in range(DC):
                        if i == 0:
                            pe.wait_ge(s.h_ready, 2 * DC * l + c + 1)
                        mm = pe.matmul(bank[b][:, 0:T], w[:, c, :], hT[:, c, :], start=(c == 0), stop=(c == DC - 1))
                    mm.then_inc(s.pages_used, 1)

                for i in range(ZC + GC):
                    z(i)
                    if 8 <= i < 16:
                        j = i - 8
                        pe.wait_ge(s.qk_square, 8 * l + j + 1)
                        if j >= 2:
                            pe.wait_ge(s.qk_root, 8 * l + j - 1)
                        pe.matmul(bank[6 + j % 2][:, 0:T], halves, sq[:, j, :], start=True, stop=True).then_inc(s.qk_sum_mm, 1)
                    if i == 22:
                        pe.wait_ge(s.qk_ready, 8 * (l + 1))
                        pe.wait_ge(s.mod_out, 2 * l + 1)
                        for h in range(H):
                            t = pe.transpose(bank[0][0:NS, h * P:(h + 1) * P], ATT["q_s"][:, h, :], ident)
                        t.then_inc(s.qs_mm, 1)
                        for h in range(H):
                            t = pe.transpose(bank[1][0:NS, h * P:(h + 1) * P], ATT["kT"][:, h, S:T], ident)
                        t.then_inc(s.qs_mm, 1)
                    if i >= 24:
                        b = i - 24
                        if b == 0:
                            pe.wait_ge(s.ks_ready, l + 1)
                        if b >= 2:
                            pe.wait_ge(s.raw_ready, NS * l + b - 1)
                        pe.matmul(bank[6 + b % 2][:, :], cst[0:NS, CO["pick"][0] + b * P:CO["pick"][0] + (b + 1) * P],
                                  ATT["qs_tok"], start=True, stop=True).then_inc(s.spread_mm, 1)

                def by_tokens(b, src, i):
                    for h in range(H):
                        t = pe.transpose(bank[b][:, h * P:(h + 1) * P], src[:, h, i * P:(i + 1) * P], ident)
                    return t

                by_tokens(0, ATT["vT"], 0).then_inc(s.v_mm, 1)
                by_tokens(1, ATT["vT"], 1).then_inc(s.v_mm, 1)
                pe.wait_ge(s.raw_ready, NS * (l + 1))
                by_tokens(6, ATT["kT"], 0).then_inc(s.k_mm, 1)
                by_tokens(7, ATT["kT"], 1).then_inc(s.k_mm, 1)

                def score(n):
                    h, i = n // 2, n % 2
                    w = P * (i + 1)
                    if n < 4:
                        pe.wait_ge(s.gate_out, GC * l + 12 + n + 1)
                    else:
                        pe.wait_ge(s.score_out, 8 * l + n - 3)
                    for m in range(2):
                        mm = pe.matmul(bank[2 + n % 4][:, m * S:m * S + w], ATT["qz"][:, m, h, i * P:(i + 1) * P],
                                       ATT["kT"][:, h, 0:w], start=True, stop=True)
                    mm.then_inc(s.score_mm, 1)

                for n in range(4):
                    score(n)
                pe.wait_ge(s.v_out, 2 * l + 1)
                for h in range(H):
                    t = pe.transpose(bank[0][0:NS, h * P:(h + 1) * P], ATT["vT"][:, h, S:T], ident)
                t.then_inc(s.vs_mm, 1)
                pe.wait_ge(s.v_out, 2 * l + 2)
                pe.wait_ge(s.v_out_u, l + 1)
                for g in range(H):
                    t = pe.transpose(bank[1][0:23, g * P:(g + 1) * P], ATT["u_last"][:, g, :], ident)
                t.then_inc(s.us_mm, 1)
                pe.wait_ge(s.k_out, 2 * l + 1)
                for j in range(PAGES):
                    pe.transpose(bank[6][0:64, j * P:(j + 1) * P], ATT["raw_s"][:, j, :], ident)
                pe.matmul(bank[6][0:64, PAST:PAST + 1], ATT["new_d"].rearrange("p a b -> p (a b)"), ones[0:NS, 0:1],
                          start=True, stop=True).then_inc(s.raw_s_mm, 1)

                def turn(h):
                    if h == 0:
                        pe.wait_ge(s.vs_out, l + 1)
                    elif h >= 2:
                        pe.wait_ge(s.aT_out, 4 * l + h - 1)
                    pe.wait_ge(s.a_ready, 8 * l + 2 * h + 2)
                    for at, (i, kb) in enumerate(((0, 0), (1, 0), (1, 1))):
                        t = pe.transpose(bank[h % 2][:, at * P:(at + 1) * P], ATT["a"][:, i, kb * P:(kb + 1) * P], ident)
                    t.then_inc(s.a_mm, 1)

                def output(h):
                    if h:
                        pe.wait_ge(s.o_out, 4 * l + h)
                    pe.wait_ge(s.aT_out, 4 * l + h + 1)
                    pe.matmul(bank[6][:, 0:S], ATT["v_tok"][:, 0, h * P:(h + 1) * P], ATT["aT"][:, h % 2, 0:S],
                              start=True, stop=False, skip_group_check=True)
                    pe.matmul(bank[6][:, P:S], ATT["v_tok"][:, 1, h * P:(h + 1) * P], ATT["aT"][:, h % 2, S:S + P],
                              start=False, stop=True, skip_group_check=True).then_inc(s.av_mm, 1)

                turn(0)
                pe.wait_ge(s.k_out, 2 * l + 2)
                pe.wait_ge(s.us_out, l + 1)
                pe.wait_ge(s.raw_s_out, l + 1)
                modulation(7, 32, (1, 6), 12 * l + 4)
                score(4)
                score(5); turn(1); output(0)
                score(6); turn(2); output(1)
                score(7); turn(3); output(2); output(3)

                pe.wait_ge(s.prob_s_ready, l + 1)
                pe.wait_ge(s.score_out, 8 * (l + 1))
                for j in range(PAGES):
                    pe.matmul(bank[2][:, 32 * j:32 * j + 32], ATT["prob_s"][:, j * P:(j + 1) * P], comb_m[:, :],
                              start=True, stop=True)
                pe.matmul(bank[2][:, 64:96], ATT["new_wide"], comb_m[:, :], start=True, stop=True).then_inc(s.a_s_mm, 1)
                pe.wait_ge(s.a_s_out, l + 1)
                for i in range(NS * PAGES):
                    b, j = i // PAGES, i % PAGES
                    n = 2 * NS * PAGES * l + NS * PAGES + i
                    pe.wait_ge(kv_in[n % KV_RING], 16 * (n // KV_RING + 1))
                    for h in range(H):
                        mm = pe.matmul(bank[3][:, 32 * j + h * NS + b:32 * j + h * NS + b + 1],
                                       ATT["kv"][:, n % KV_RING, h * P:(h + 1) * P],
                                       ATT["a_s"][:, 32 * j + h * NS + b:32 * j + h * NS + b + 1],
                                       start=True, stop=True)
                    mm.then_inc(s.kv_used, 1)

                for h in range(H):
                    pe.wait_ge(s.o_square, 4 * l + h + 1)
                    if h >= 2:
                        pe.wait_ge(s.o_root, 4 * l + h - 1)
                    pe.matmul(bank[4 + h % 2][:, 0:T], ones, o_sq[:, h % 2, :], start=True, stop=True).then_inc(s.o_sum_mm, 1)
                for g in range(H):
                    if g == 0:
                        pe.wait_ge(s.w_pool_in, 16 * (l + 1))
                        pe.wait_ge(s.d_ready, l + 1)
                        pe.wait_ge(s.aT_out, 4 * (l + 1))
                    if g >= 2:
                        pe.wait_ge(s.y_ready, 4 * l + g - 1)
                    pe.matmul(bank[g % 2][:, 0:T], w_pool[:, g, :], ATT["yT"][:, g, :], start=True, stop=True).then_inc(s.pool_mm, 1)

                pe.wait_ge(s.y_ready, 4 * (l + 1))
                pe.wait_ge(s.o_ready, 4 * (l + 1))
                pe.wait_ge(s.o_s_out, l + 1)
                for j in range(8):
                    if j >= 2:
                        pe.wait_ge(s.branch_out, 8 * l + j - 1)
                    w = page()
                    for half, x in ((0, oT), (1, ATT["yT"])):
                        for c in range(H):
                            mm = pe.matmul(bank[2 + 2 * (j % 2) + half][:, 0:T], w[:, 4 * half + c, :], x[:, c, :],
                                           start=(c == 0), stop=(c == H - 1))
                    mm.then_inc(s.pages_used, 1)
                out_bank = (0, 1, 6)
                pe.wait_ge(s.mod_out, 2 * l + 2)
                for j in range(8):
                    if j >= 3:
                        pe.wait_ge(s.x_new, 2 * DC * l + j - 2)
                    w = page()
                    for c in range(DC):
                        if j == 0:
                            pe.wait_ge(s.branch_out, 8 * l + c + 1)
                        mm = pe.matmul(bank[out_bank[j % 3]][:, 0:T], w[:, c, :], hT[:, c, :], start=(c == 0), stop=(c == DC - 1))
                    mm.then_inc(s.pages_used, 1)

                pe.wait_ge(s.x_new, 2 * DC * l + DC)
                sums(2 * l + 1)
                pe.wait_ge(s.h_ready, 2 * DC * (l + 1))

                def gate_up(c, k, w, x, n):
                    for half, read in ((0, s.silu_out), (1, s.act_out)):
                        if c >= 2 or not isinstance(k, int) or k:
                            pe.wait_ge(read, k + max(c - 1, 0))
                        column(bank[2 * half + c % 2][:, 0:n], w(2 * c + half), x)

                def full_down(n, k, adds, w):
                    downs = [w(2 * n + c) for c in range(n)]
                    for j in range(DC):
                        if j >= 4 or not isinstance(adds, int) or adds:
                            pe.wait_ge(s.y_added, adds + max(j - 3, 0))
                        for c in range(n):
                            if j == 0:
                                pe.wait_ge(s.act_out, k + (c + 1))
                            mm = pe.matmul(bank[4 + j % 4][:, 0:T], downs[c][:, j, :], FFN["act"][:, c, :],
                                           start=(c == 0), stop=(c == n - 1))
                            if j == DC - 1:
                                mm.then_inc(s.pages_used, 1)
                        if j < DC - 1:
                            mm.then_inc(s.y_mm, 1)

                if l == 0:
                    k = 0
                    for i, n in enumerate(FF_GROUPS):
                        for c in range(n):
                            gate_up(c, k, lambda _: page(), hT, T)
                        full_down(n, k, DC * i, lambda _: page())
                        k += n
                    pe.wait_ge(s.x_new, 2 * DC)

            for i in range(3):
                rows = min(P, T - i * P)
                for half in range(2):
                    n = 2 * i + half
                    if n >= 2:
                        pe.wait_ge(s.h_tok_out, n - 1)
                    for c in range(4):
                        t = pe.transpose(bank[4 + n % 2][0:rows, c * P:(c + 1) * P],
                                         hT[:, 4 * half + c, i * P:i * P + rows], ident)
                    t.then_inc(s.h_tok_mm, 1)
            for i in range(3):
                rows = min(P, T - i * P)
                for c in range(DC):
                    mm = pe.matmul(bank[6][0:rows, i * E:(i + 1) * E], hT[:, c, i * P:i * P + rows], w_route[:, c, :],
                                   start=(c == 0), stop=(c == DC - 1))
            mm.then_inc(s.route_mm, 1)
            pe.wait_ge(s.sel_ready, 1)
            for i in range(3):
                for j in range(i + 1):
                    pe.matmul(bank[7][:, i * E:(i + 1) * E], before if j == i else ones, FFN["sel"][:, j, 0:E],
                              start=(j == 0), stop=(j == i))
            for j in range(3):
                mm = pe.matmul(bank[7][:, 3 * E:4 * E], ones, FFN["sel"][:, j, 0:E], start=(j == 0), stop=(j == 2))
            mm.then_inc(s.rank_mm, 1)
            pe.wait_ge(s.routed, 1)
            pe.wait_ge(s.h_tok_out, 6)

            def prepare(e, count):
                pe.wait_ge(s.got_ready, e + 1)
                with pe.If(count < CAP + 1):
                    for c in range(DC):
                        for i in range(3):
                            rows = min(P, T - i * P)
                            mm = pe.matmul(bank[6 + c // 4][:, (c % 4) * CAP:(c % 4 + 1) * CAP],
                                           FFN["h_tok"][0:rows, i, c * P:(c + 1) * P], FFN["got"][0:rows, i, :],
                                           start=(i == 0), stop=(i == 2))
                        if c % 4 == 3:
                            mm.then_inc(s.h_got_mm, 1)
                    for i in range(3):
                        rows = min(P, T - i * P)
                        t = pe.transpose(bank[2][0:CAP, i * P:i * P + rows], FFN["got_w"][0:rows, i, :], ident[0:rows, 0:rows])
                    t.then_inc(s.put_mm, 1)
                with pe.Else():
                    for i in range(3):
                        rows = min(P, T - i * P)
                        mm = pe.matmul(bank[2][:, i * P:i * P + rows], FFN["cmb_wide"][0:rows, i, :], ident[0:rows, 0:rows],
                                       start=True, stop=True)
                    mm.then_inc(s.put_mm, 1)
                    pe.sem_inc(s.h_got_mm, 2)

            def load_count(e):
                return pe.value_load(count_i[0:1, bass.ds(e, 1)], min_val=0, max_val=T)

            pe.wait_ge(s.f_added, 1)
            prepare(0, pe.value_load(count_i[0:1, 0:1], min_val=0, max_val=T))
            with pe.Fori(0, E) as e:
                count = load_count(e)
                with pe.If(count < CAP + 1):
                    pe.wait_ge(s.put_out, e + 1)
                    pe.wait_ge(s.h_got_out, e * 2 + 2)
                    for y in range(2):
                        pe.matmul(bank[4 + y][:, 0:4 * CAP], zeros[:, 0:P], zeros[:, 0:4 * CAP], start=True, stop=True)
                with pe.Fori(0, BODIES) as b:
                    n = e * BODIES + b

                    def w(i):
                        at = eslot[i]
                        pe.wait_ge(page_in[at], n * 16 + (landed[at] + 16))
                        return slot(at)

                    k = n * BODY + DENSE_CHUNKS
                    with pe.If(count < CAP + 1):
                        for c in range(BODY):
                            gate_up(c, k, w, FFN["h_got"], CAP)
                        for c in range(BODY):
                            down = w(2 * BODY + c)
                            pe.wait_ge(s.act_out, k + (c + 1))
                            for j in range(DC):
                                mm = pe.matmul(bank[4 + j // 4][:, (j % 4) * CAP:(j % 4 + 1) * CAP], down[:, j, :],
                                               FFN["act"][:, c, 0:CAP], start=False, stop=False, skip_group_check=True)
                            mm.then_inc(s.pages_used, 1)
                        pe.sem_inc(s.y_mm, DC - 1)
                    with pe.Else():
                        pe.wait_ge(s.put_out, e + 1)
                        for c in range(BODY):
                            gate_up(c, k, w, hT, T)
                        pe.wait_ge(s.f_added, e * DC + 1)
                        full_down(BODY, k, n * DC + len(FF_GROUPS) * DC, w)
                pe.wait_ge(s.act_out, (e + 1) * (BODIES * BODY) + DENSE_CHUNKS)
                pe.wait_ge(s.y_added, (e + 1) * (BODIES * DC) + len(FF_GROUPS) * DC)
                pe.wait_ge(s.f_added, e * DC + 1)
                prepare(e + 1, load_count(e + 1))
                with pe.If(count < CAP + 1):
                    for half in range(2):
                        pe.wait_ge(s.yT_out, e * 2 + half + 1)
                        for c in range(4):
                            t = pe.transpose(bank[half][0:CAP, c * P:(c + 1) * P], FFN["y"][:, 4 * half + c, :], ident)
                        t.then_inc(s.yT_mm, 1)
                    pe.wait_ge(s.h_got_out, e * 2 + 4)
                    pe.wait_ge(s.put_kept, e + 1)
                    for c in range(DC):
                        if c % 4 == 0:
                            pe.wait_ge(s.y_tok_out, e * 2 + c // 4 + 1)
                        if c >= 2:
                            pe.wait_ge(s.f_added, e * DC + c)
                        pe.matmul(bank[6 + c % 2][:, 0:T], FFN["y_tok"][:, c * P:(c + 1) * P], FFN["put"],
                                  start=True, stop=True).then_inc(s.put_y_mm, 1)
                with pe.Else():
                    pe.sem_inc(s.yT_mm, 2)
                    pe.sem_inc(s.put_y_mm, DC)

            pe.wait_ge(s.x_new, 4 * DC)
            for i in range(3):
                rows = min(P, T - i * P)
                for half in range(2):
                    for c in range(4):
                        t = pe.transpose(bank[2 * i + half][0:rows, c * P:(c + 1) * P],
                                         xT[:, 4 * half + c, i * P:i * P + rows], ident)
                    t.then_inc(s.final_mm, 1)

        @block.vector
        def _(dve):
            step = Step(dve, s.dve_step)

            def wide(v, shape):
                return v.to_broadcast(list(shape))

            dve.memset(eps[:, :], EPS).then_inc(s.dve_step, 1)
            dve.memset(zero[:, :], 0.0).then_inc(s.dve_step, 1)
            dve.memset(zeros[:, :], 0.0).then_inc(s.dve_step, 1)
            step.n = 3
            dve.wait_ge(s.dve_step, 3)
            step(dve.memset(PRO["rb"][BUCKETS:BUCKETS + 1, :], MASKED))
            step(dve.memset(cT[:, :, :], 0.0))
            dve.wait_ge(s.c_mm, 1)
            dve.tensor_copy(cT[:, :, 0:NC], bank[1][:, 0:DC * NC].rearrange("p (c n) -> p c n", c=DC)).then_inc(s.c_out, 1)
            dve.wait_ge(s.inputs_in, INPUTS)
            dve.wait_ge(s.tokens_in, 16 * 3)
            step(dve.tensor_copy(PRO["rb_rows"].rearrange("p (b h m) -> p b h m", b=NS, h=H),
                                 PRO["rb"].unsqueeze(1).unsqueeze(3).broadcast_to([BUCKETS + 1, NS, H, 2])))
            dve.tensor_copy(PRO["rb_wide"], PRO["rb"].unsqueeze(2).broadcast_to([BUCKETS + 1, H, P])).then_inc(s.wide_ready, 1)
            lam_in = PRO["lam_in"]
            step(dve.tensor_tensor(PRO["lam_prod"], lam_in[:, :, 0, :], lam_in[:, :, 1, :], ALU.mult))
            dve.tensor_reduce(lam[:, :], PRO["lam_prod"], AX.X, ALU.add).then_inc(s.lam_ready, 1)
            dve.wait_ge(s.vec_mm, 1)
            dve.tensor_copy(vecT[:, :], bank[1][:, 0:142]).then_inc(s.vec_out, 1)
            dve.wait_ge(s.vec_out, 1)
            for l in range(LAYERS):
                step(dve.tensor_scalar(sub_gain[:, l:l + 1], vecT[:, 136 + l:137 + l], 1.0 - LAM_INIT[l], None, ALU.mult))
            for c in range(DC):
                dve.wait_ge(s.x_mm, c + 1)
                dve.tensor_copy(xT[:, c, :], bank[2 + c % 4][:, 0:T]).then_inc(s.x_out, 1)
            for h in range(H):
                dve.wait_ge(s.bias_mm, h + 1)
                dve.tensor_copy(PRO["bias_row"][:, h, :], bank[6 + h % 2][:, 0:WL]).then_inc(s.bias_out, 1)
            dve.wait_ge(s.bias_mm, H + 1)
            dve.tensor_copy(bias_s[:, :], bank[1][0:64, 0:PAST + 1]).then_inc(s.bias_out, 1)
            dve.wait_ge(s.lam_exp, 1)
            for l in range(LAYERS):
                step(dve.tensor_tensor(neglam[:, l:l + 1], lam[:, 2 * l + 1:2 * l + 2], lam[:, 2 * l:2 * l + 1], ALU.subtract))
                step(dve.tensor_scalar(neglam[:, l:l + 1], neglam[:, l:l + 1], -LAM_INIT[l], None, ALU.add))
            for l in range(LAYERS):
                dve.wait_ge(s.state_mm, l + 1)
                for g, w in enumerate(WINDOWS):
                    rows = bank[4 + l][:, g * 120:(g + 1) * 120].rearrange("p (b r) -> p b r", b=NS)[:, :, BUF - (w - 1):BUF]
                    r = dve.tensor_reduce(state_sum[:, l, g, :], rows, AX.X, ALU.add)
                    if g < H - 1:
                        step(r)
                    else:
                        r.then_inc(s.state_out, 1)
            dve.wait_ge(s.state_out, LAYERS)

            def norm(l, which):
                n = 2 * l + which
                sh, sc = mod[:, 24 * which:24 * which + 8, :], mod[:, 24 * which + 8:24 * which + 16, :]
                g = vecT[:, (96, 112)[which] + 8 * l:(96, 112)[which] + 8 * l + 8]
                if n:
                    dve.wait_ge(s.h_ready, DC * n)
                if which:
                    dve.wait_ge(s.o_ready, H * (l + 1))
                step(dve.scalar_tensor_tensor(out=gain[:, :, :], in0=sc, scalar=1.0,
                                              in1=g.unsqueeze(2).broadcast_to([P, DC, NC]), op0=ALU.add, op1=ALU.mult))
                dve.wait_ge(s.root_out, n + 1)
                step(dve.reciprocal(inv[:, :], root[:, 0, :]))
                step(dve.tensor_tensor(hT[:, :, :], xT[:, :, :], inv[:, :].unsqueeze(1).broadcast_to([P, DC, T]), ALU.mult))
                step(dve.tensor_tensor(hT[:, :, S:T], hT[:, :, S:T], gain[:, :, 1:NC], ALU.mult))
                step(dve.tensor_tensor(hT[:, :, S:T], hT[:, :, S:T], sh[:, :, 1:NC], ALU.add))
                for c in range(DC):
                    dve.tensor_scalar(hT[:, c, 0:S], hT[:, c, 0:S], gain[:, c, 0:1], sh[:, c, 0:1],
                                      ALU.mult, ALU.add).then_inc(s.h_ready, 1)

            for l in range(LAYERS):
                L = layer_page(l)
                if l:
                    dve.wait_ge(s.x_new, 2 * DC * l)
                dve.wait_ge(s.mod_mm, 12 * l + 4)
                dve.tensor_tensor(mod[:, 0:16, :], bank[0][:, 0:16 * NC].rearrange("p (c n) -> p c n", c=16),
                                  vecT[:, 48 * l:48 * l + 16].unsqueeze(2).broadcast_to([P, 16, NC]),
                                  ALU.add).then_inc(s.mod_out, 1)
                dve.wait_ge(s.mod_out, 2 * l + 1)
                norm(l, 0)
                step(dve.scalar_tensor_tensor(out=comb_m[:, :], in0=const("comb_b", 64), scalar=neglam[0:64, l:l + 1],
                                              in1=const("comb_a", 64), op0=ALU.mult, op1=ALU.add))
                if l:
                    dve.wait_ge(s.pooled, 1)
                else:
                    dve.wait_ge(s.bias_wrote, 16)
                    dve.wait_ge(s.bias_mm, H + 1)

                step(dve.memset(ATT["qz"][HD:P, 0, :, :], 0.0))
                step(dve.memset(ATT["qz"][0:HD, 1, :, :], 0.0))
                step(dve.memset(ATT["u_ext"][:, :, 0:BUF], 0.0))

                def read_z(i):
                    dve.wait_ge(s.pages_used, L + 16 + i + 1)
                    z, b = i % QC, bank[2 + i % 4]
                    if i < 12:
                        dst = (ATT["q_raw"], ATT["kT"], ATT["vT"])[i // QC]
                        dve.tensor_copy(dst[:, z, :], b[:, 0:T]).then_inc(s.z_out, 1)
                    else:
                        step(dve.tensor_copy(ATT["u_ext"][:, z, BUF:BUF + S], b[:, 0:S]))
                        dve.tensor_copy(ATT["u_s"][:, z, :], b[:, S:T]).then_inc(s.z_out, 1)

                def norm_qk(i):
                    dve.wait_ge(s.qk_root, 8 * l + i + 1)
                    dve.wait_ge(s.qk_ready, 8 * l + i) if i else dve.wait_ge(s.h_ready, DC * (2 * l + 1))
                    step(dve.reciprocal(inv[:, :], root[:, i % 2, :]))
                    g = vecT[:, (138, 140)[i // QC] + l:(138, 140)[i // QC] + l + 1]
                    if i >= QC:
                        k = ATT["kT"][:, i - QC, :]
                        dve.scalar_tensor_tensor(out=k, in0=k, scalar=g, in1=inv[:, :], op0=ALU.mult,
                                                 op1=ALU.mult).then_inc(s.qk_ready, 1)
                        return
                    q = ATT["q_raw"][:, i, :]
                    for m in range(2):
                        r = slice(m * HD, (m + 1) * HD)
                        step(dve.scalar_tensor_tensor(out=ATT["qz"][r, m, i, :], in0=q[r, 0:S], scalar=g[r, :],
                                                      in1=inv[r, 0:S], op0=ALU.mult, op1=ALU.mult))
                    dve.scalar_tensor_tensor(out=ATT["q_s"][:, i, :], in0=q[:, S:T], scalar=g, in1=inv[:, S:T],
                                             op0=ALU.mult, op1=ALU.mult).then_inc(s.qk_ready, 1)

                for i in range(ZC):
                    read_z(i)
                    if i >= 9:
                        norm_qk(i - 9)
                norm_qk(7)

                dve.wait_ge(s.qs_mm, 2 * l + 1)
                step(dve.tensor_copy(ATT["qs_tok"], bank[0][0:NS, :]))
                dve.wait_ge(s.qs_mm, 2 * l + 2)
                dve.tensor_copy(ATT["ks_tok"], bank[1][0:NS, :]).then_inc(s.ks_ready, 1)
                dve.wait_ge(s.ks_ready, l + 1)
                step(dve.tensor_tensor(ATT["prod"][0:NS, :], ATT["qs_tok"], ATT["ks_tok"], ALU.mult))
                step(dve.tensor_reduce(ATT["new_s"], ATT["prod"][0:NS, :].rearrange("p (g d) -> p g d", g=8), AX.X, ALU.add))
                step(dve.tensor_tensor(ATT["new_d"], ATT["new_s"].unsqueeze(1).broadcast_to([NS, NS, NS]),
                                       ident[0:NS, 0:NS].unsqueeze(2).broadcast_to([NS, NS, NS]), ALU.mult))

                for b in range(NS):
                    dve.wait_ge(s.spread_mm, NS * l + b + 1)
                    for j in range(PAGES):
                        n = 2 * NS * PAGES * l + b * PAGES + j
                        dve.wait_ge(kv_in[n % KV_RING], 16 * (n // KV_RING + 1))
                        dve.tensor_tensor(ATT["prod"], ATT["kv"][:, n % KV_RING, :], bank[6 + b % 2][:, :],
                                          ALU.mult).then_inc(s.kv_used, 1)
                        dve.wait_ge(s.kv_used, n + 1)
                        r = dve.tensor_reduce(ATT["raw_s"][:, j, 8 * b:8 * b + 8], ATT["prod"].rearrange("p (g d) -> p g d", g=8),
                                              AX.X, ALU.add)
                        if j == 0:
                            step(r)
                        else:
                            r.then_inc(s.raw_ready, 1)
                    dve.wait_ge(s.raw_ready, NS * l + b + 1)
                for i in range(2):
                    dve.wait_ge(s.v_mm, 2 * l + i + 1)
                    dve.tensor_copy(ATT["v_tok"][:, i, :], bank[i][:, :]).then_inc(s.v_out, 1)
                step(dve.tensor_copy(ATT["u_last"][:, :, 0:BUF], ATT["u_ext"][:, :, S:BUF + S]))
                dve.tensor_copy(ATT["u_last"][:, :, BUF:23], ATT["u_s"]).then_inc(s.v_out_u, 1)

                def pooling():
                    u, d = ATT["u_ext"], ATT["yT"]
                    n = BUF + S
                    step(dve.tensor_tensor(scr_a[:, :, 1:n], u[:, :, 1:n], u[:, :, 0:n - 1], ALU.add))
                    step(dve.tensor_tensor(scr_b[:, :, 3:n], scr_a[:, 1:4, 3:n], scr_a[:, 1:4, 1:n - 2], ALU.add))
                    step(dve.tensor_tensor(scr_a[:, 2:4, 7:n], scr_b[:, 1:3, 7:n], scr_b[:, 1:3, 3:n - 4], ALU.add))
                    step(dve.tensor_tensor(scr_b[:, 2:3, 15:n], scr_a[:, 3:4, 15:n], scr_a[:, 3:4, 7:n - 8], ALU.add))
                    total = (scr_a[:, 0, :], scr_b[:, 0, :], scr_a[:, 2, :], scr_b[:, 2, :])
                    for g, w in enumerate(WINDOWS):
                        step(dve.scalar_tensor_tensor(out=d[:, g, 16:S], in0=total[g][:, BUF + 16:n], scalar=1.0 / w,
                                                      in1=u[:, g, BUF + 16:n], op0=ALU.mult, op1=ALU.subtract))
                        step(dve.tensor_tensor(d[:, g, 0:16], total[g][:, BUF:BUF + 16], inv_count[:, g, :], ALU.mult))
                        step(dve.tensor_tensor(d[:, g, 0:16], d[:, g, 0:16], u[:, g, BUF:BUF + 16], ALU.subtract))
                        step(dve.tensor_tensor(d[:, g, S:T], state_sum[:, l, g, :], ATT["u_s"][:, g, :], ALU.add))
                        r = dve.scalar_tensor_tensor(out=d[:, g, S:T], in0=d[:, g, S:T], scalar=1.0 / w,
                                                     in1=ATT["u_s"][:, g, :], op0=ALU.mult, op1=ALU.subtract)
                        if g < H - 1:
                            step(r)
                        else:
                            r.then_inc(s.d_ready, 1)

                def scores(n):
                    h, i = n // 2, n % 2
                    w = P * (i + 1)
                    prob = ATT["prob"][:, 2 * (n % 2):2 * (n % 2) + 2, 0:w]
                    top = ATT["top"][:, 2 * (n % 2):2 * (n % 2) + 2]
                    dve.wait_ge(s.score_mm, 8 * l + n + 1)
                    if n >= 2:
                        dve.wait_ge(s.a_ready, 8 * l + n - 1)
                    dve.scalar_tensor_tensor(out=prob, in0=bank[2 + n % 4][:, :].rearrange("p (m k) -> p m k", m=2)[:, :, 0:w],
                                             scalar=SCALE, in1=bias[:, h, S - w:S].unsqueeze(1).broadcast_to([P, 2, w]),
                                             op0=ALU.mult, op1=ALU.add).then_inc(s.score_out, 1)
                    dve.wait_ge(s.score_out, 8 * l + n + 1)
                    step(dve.tensor_reduce(top, prob, AX.X, ALU.max))
                    dve.tensor_scalar(top, top, -1.0, None, ALU.mult).then_inc(s.top_ready, 1)

                def weights(n):
                    w = P * (n % 2 + 1)
                    prob = ATT["prob"][:, 2 * (n % 2):2 * (n % 2) + 2, 0:w]
                    total, rec = ATT["sum"][:, 2 * (n % 2):2 * (n % 2) + 2], ATT["rec"][:, 2 * (n % 2):2 * (n % 2) + 2]
                    dve.wait_ge(s.exp_out, 2 * (8 * l + n + 1))
                    step(dve.reciprocal(rec, total))
                    step(dve.tensor_tensor(rec[:, 1:2], rec[:, 1:2], neglam[:, l:l + 1], ALU.mult))
                    step(dve.tensor_scalar(prob[:, 0, :], prob[:, 0, :], rec[:, 0:1], None, ALU.mult))
                    if n >= 2:
                        dve.wait_ge(s.a_mm, 4 * l + n // 2)
                    dve.scalar_tensor_tensor(out=ATT["a"][:, n % 2, 0:w], in0=prob[:, 1, :], scalar=rec[:, 1:2],
                                             in1=prob[:, 0, :], op0=ALU.mult, op1=ALU.add).then_inc(s.a_ready, 1)

                def read_o(h):
                    dve.wait_ge(s.av_mm, 4 * l + h + 1)
                    dve.tensor_copy(oT[:, h, 0:S], bank[6][:, 0:S]).then_inc(s.o_out, 1)

                scores(0); scores(1); weights(0); scores(2); weights(1); scores(3)
                dve.wait_ge(s.vs_mm, l + 1)
                dve.tensor_copy(ATT["vs_tok"], bank[0][0:NS, :]).then_inc(s.vs_out, 1)
                dve.wait_ge(s.us_mm, l + 1)
                dve.tensor_copy(ATT["u_tok"], bank[1][0:23, :]).then_inc(s.us_out, 1)
                prob_s, top_s = ATT["prob_s"], ATT["top_s"]
                dve.wait_ge(s.raw_s_mm, l + 1)
                dve.scalar_tensor_tensor(out=prob_s, in0=bank[6][0:64, 0:PAST + 1], scalar=SCALE, in1=bias_s[:, :],
                                         op0=ALU.mult, op1=ALU.add).then_inc(s.raw_s_out, 1)
                dve.wait_ge(s.raw_s_out, l + 1)
                step(dve.tensor_reduce(top_s[:, 0:1], prob_s, AX.X, ALU.max))
                dve.tensor_scalar(top_s[:, 1:2], top_s[:, 0:1], -1.0, None, ALU.mult).then_inc(s.top_s_ready, 1)
                weights(2); scores(4); weights(3)
                dve.wait_ge(s.exp_s_out, l + 1)
                step(dve.reciprocal(top_s[:, 3:4], top_s[:, 2:3]))
                step(dve.tensor_scalar(prob_s, prob_s, top_s[:, 3:4], None, ALU.mult))
                dve.tensor_copy(ATT["new_wide"], prob_s[:, PAST:PAST + 1].to_broadcast([64, P])).then_inc(s.prob_s_ready, 1)
                scores(5); weights(4); scores(6); weights(5); read_o(0)
                scores(7); weights(6); read_o(1); weights(7); read_o(2); read_o(3)
                dve.wait_ge(s.a_s_mm, l + 1)
                dve.tensor_copy(ATT["a_s"], bank[2][:, 0:96]).then_inc(s.a_s_out, 1)
                dve.wait_ge(s.mod_mm, 12 * (l + 1))
                dve.tensor_tensor(mod[:, 16:48, :], bank[7][:, 0:32 * NC].rearrange("p (c n) -> p c n", c=32),
                                  vecT[:, 48 * l + 16:48 * l + 48].unsqueeze(2).broadcast_to([P, 32, NC]),
                                  ALU.add).then_inc(s.mod_out, 1)
                pooling()
                dve.wait_ge(s.kv_used, 2 * NS * PAGES * (l + 1))
                dve.wait_ge(s.a_s_out, l + 1)
                tmp = ATT["tmp_s"][:, 0:H, :]
                new = ATT["a_s"][:, 64:96].rearrange("p (h b) -> p h b", h=H)
                o_s = oT[:, :, S:T]
                step(dve.tensor_tensor(tmp, ATT["vT"][:, :, S:T], new, ALU.mult))
                for j in range(PAGES):
                    r = dve.tensor_tensor(tmp if j == 0 else o_s, bank[3][:, 32 * j:32 * j + 32].rearrange("p (h b) -> p h b", h=H),
                                          tmp, ALU.add)
                    if j == 0:
                        step(r)
                    else:
                        r.then_inc(s.o_s_out, 1)
                dve.wait_ge(s.o_s_out, l + 1)
                for h in range(H):
                    dve.wait_ge(s.o_root, 4 * l + h + 1)
                    dve.wait_ge(s.o_ready, H * l + h) if h else dve.wait_ge(s.qk_ready, 8 * (l + 1))
                    step(dve.reciprocal(inv[:, :], root[:, h % 2, :]))
                    dve.scalar_tensor_tensor(out=oT[:, h, :], in0=oT[:, h, :], scalar=sub_gain[:, l:l + 1], in1=inv[:, :],
                                             op0=ALU.mult, op1=ALU.mult).then_inc(s.o_ready, 1)
                for j in range(8):
                    dve.wait_ge(s.pages_used, L + 80 + j + 1)
                    dve.wait_ge(s.gate_out, GC * (l + 1))
                    b = 2 + 2 * (j % 2)
                    step(dve.tensor_tensor(hT[:, j, :], bank[b][:, 0:T], ATT["gate"][:, j, :], ALU.mult))
                    step(dve.tensor_tensor(ATT["gate"][:, 8 + j, :], bank[b + 1][:, 0:T], ATT["gate"][:, 8 + j, :], ALU.mult))
                    dve.tensor_tensor(hT[:, j, :], hT[:, j, :], ATT["gate"][:, 8 + j, :], ALU.add).then_inc(s.branch_out, 1)
                for j in range(8):
                    dve.wait_ge(s.pages_used, L + 88 + j + 1)
                    b = bank[(0, 1, 6)[j % 3]]
                    step(dve.tensor_tensor(ATT["tmp_s"][:, j, :], b[:, S:T], mod[:, 16 + j, 1:NC], ALU.mult))
                    step(dve.tensor_tensor(xT[:, j, S:T], xT[:, j, S:T], ATT["tmp_s"][:, j, :], ALU.add))
                    dve.scalar_tensor_tensor(out=xT[:, j, 0:S], in0=b[:, 0:S], scalar=mod[:, 16 + j, 0:1],
                                             in1=xT[:, j, 0:S], op0=ALU.mult, op1=ALU.add).then_inc(s.x_new, 1)
                dve.wait_ge(s.x_new, 2 * DC * l + DC)
                norm(l, 1)
                dve.wait_ge(s.pooled, l + 1)
                f = FFN["fT"]
                act_t, silu = FFN["act"], FFN["silu"]
                if l == 0:
                    step(dve.memset(f, 0.0))
                    k, at = 0, LAYER_PAGES
                    for i, n in enumerate(FF_GROUPS):
                        for c in range(n):
                            dve.wait_ge(s.silu_out, k + 1)
                            dve.wait_ge(s.pages_used, at + 2 * c + 2)
                            dve.tensor_tensor(act_t[:, c, :], bank[2 + c % 2][:, 0:T], silu[:, c, :],
                                              ALU.mult).then_inc(s.act_out, 1)
                            k += 1
                        for j in range(DC):
                            if j < DC - 1:
                                dve.wait_ge(s.y_mm, (DC - 1) * i + j + 1)
                            else:
                                dve.wait_ge(s.pages_used, at + 3 * n)
                            if i:
                                dve.wait_ge(s.y_added, DC * (i - 1) + j + 1)
                            dve.tensor_tensor(f[:, j, :], bank[4 + j % 4][:, 0:T], f[:, j, :], ALU.add).then_inc(s.y_added, 1)
                        at += 3 * n
                    dve.wait_ge(s.y_added, DC * len(FF_GROUPS))
                else:
                    dve.memset(f, 0.0).then_inc(s.f_added, 1)
                    experts(dve, step, f, act_t, silu)
                tmp = FFN["tmp_s"]
                step(dve.tensor_tensor(tmp, f[:, :, S:T], mod[:, 40:48, 1:NC], ALU.mult))
                step(dve.tensor_tensor(xT[:, :, S:T], xT[:, :, S:T], tmp, ALU.add))
                for j in range(8):
                    dve.scalar_tensor_tensor(out=xT[:, j, 0:S], in0=f[:, j, 0:S], scalar=mod[:, 40 + j, 0:1],
                                             in1=xT[:, j, 0:S], op0=ALU.mult, op1=ALU.add).then_inc(s.x_new, 1)
            for i in range(3):
                rows = min(P, T - i * P)
                for half in range(2):
                    dve.wait_ge(s.final_mm, 2 * i + half + 1)
                    dve.tensor_copy(y_out[0:rows, i, half * 512:(half + 1) * 512], bank[2 * i + half][0:rows, :]).then_inc(s.final_out, 1)


_INS = ["x_prompt", "x_sample", "c_prompt", "c_sample", "cache_k", "cache_v", "state_pool", "page_table", "rel_bias",
        "w_ada", "b_ada", "g_mix", "g_ffn", "w_in", "q_norm", "k_norm", "diff_lambda", "subln", "w_pool", "pool_scale",
        "w_branch", "w_out", "w_ff_gate", "w_ff_up", "w_ff_down", "w_router", "w_exp_gate", "w_exp_up", "w_exp_down"]
_OUTS = [((1, 256, 1024), "float32"), ((8, 1, 1024), "float32"), ((2, 1, 256, 4, 2, 64), "float32"),
         ((2, 1, 256, 4, 128), "float32"), ((2, 1, 15, 512), "float32"), ((2, 8, 1, 4, 2, 64), "float32"),
         ((2, 8, 1, 4, 128), "float32"), ((2, 8, 15, 512), "float32")]


def kernel(**inputs):
    import concourse.bacc as _bacc
    from concourse.bass_utils import run_bass_kernel_spmd as _run

    nc = _bacc.Bacc("TRN2", target_bir_lowering=False, num_devices=1)
    arrays, given = {}, {}
    for name in _INS + ["constants"]:
        a = constants() if name == "constants" else np.ascontiguousarray(inputs[name])
        arrays[f"in_{name}"] = a
        given[name] = nc.dram_tensor(f"in_{name}", a.shape, mybir.dt.from_np(a.dtype), kind="ExternalInput").ap()
    outs = [nc.dram_tensor(f"out_{i}", shape, mybir.dt.from_np(np.dtype(dtype)), kind="ExternalOutput").ap()
            for i, (shape, dtype) in enumerate(_OUTS)]
    build(nc, given, outs, given["constants"])
    r = _run(nc, [arrays], core_ids=[0])
    return tuple(r.results[0][f"out_{i}"] for i in range(len(_OUTS)))
```
